# Optimizing a Trainium2 kernel written in Bass

```python
import math
import jax, jax.numpy as jnp
from jax import lax
import numpy as np

D_MODEL = 1024
BATCH = 1
SEQ = 1024
DEPTH = 1

HEAD_DIM = 64
N_HEADS_A = 8
WIDTH_A = N_HEADS_A * HEAD_DIM
DILATED_PATTERNS = ((128, 1), (512, 4), (2048, 16))
N_HEADS_B = 4
DIFF_DIM = HEAD_DIM
DIFF_V_DIM = 2 * DIFF_DIM
WIDTH_B = N_HEADS_B * DIFF_V_DIM
MIX_WIDTH = WIDTH_A + WIDTH_B
IN_PROJ_COLS = 3 * WIDTH_A + 3 * WIDTH_B
ROPE_THETA = 500000.0
ROT_DIM = HEAD_DIM // 4
BLOCK = 128
NORM_EPS = 1e-6
ATTN_SCALE = 1.0 / math.sqrt(HEAD_DIM)

PEER_HEADS = 8
N_KEYS = 128
N_EXPERTS = N_KEYS * N_KEYS
KEY_DIM = 128
PEER_TOPK = 16
TOKEN_CHUNK = 128

kernel_name = "hybrid_dilated_diffattn_peer"

def rms_norm(x, g):
    x32 = x.astype(jnp.float32)
    y = x32 * lax.rsqrt(jnp.mean(x32 * x32, axis=-1, keepdims=True) + NORM_EPS)
    return (y * g.astype(jnp.float32)).astype(x.dtype)

def rope_tables(seq_len):
    pos = jnp.arange(seq_len, dtype=jnp.float32)
    inv_freq = ROPE_THETA ** (-jnp.arange(0, ROT_DIM, 2, dtype=jnp.float32) / ROT_DIM)
    ang = pos[:, None] * inv_freq[None, :]
    return jnp.cos(ang), jnp.sin(ang)

def apply_partial_rope(x, cos, sin):
    half = ROT_DIM // 2
    shape = (x.shape[1],) + (1,) * (x.ndim - 3) + (half,)
    c = cos.reshape(shape).astype(x.dtype)
    s = sin.reshape(shape).astype(x.dtype)
    x1 = x[..., :half]
    x2 = x[..., half:ROT_DIM]
    return jnp.concatenate([x1 * c - x2 * s, x2 * c + x1 * s, x[..., ROT_DIM:]], axis=-1)

def dilated_branch(q, k, v, window, dilation):
    B, H, S, Dh = q.shape
    w_s = window // dilation
    assert w_s <= BLOCK
    chunk = dilation * BLOCK
    L_pad = -(-S // chunk) * chunk
    pad = ((0, 0), (0, 0), (0, L_pad - S), (0, 0))
    Ls = L_pad // dilation
    nb = Ls // BLOCK

    def to_blocks(a):
        a = jnp.pad(a, pad).reshape(B, H, Ls, dilation, Dh).transpose(0, 1, 3, 2, 4)
        return a.reshape(B, H, dilation, nb, BLOCK, Dh)

    def band(a):
        prev = jnp.pad(a, ((0, 0), (0, 0), (0, 0), (1, 0), (0, 0), (0, 0)))[:, :, :, :-1]
        return jnp.concatenate([prev, a], axis=4)

    qb = to_blocks(q)
    kb = band(to_blocks(k))
    vb = band(to_blocks(v))
    s = jnp.einsum('bhrnqd,bhrnkd->bhrnqk', qb, kb,
                   preferred_element_type=jnp.float32) * ATTN_SCALE
    qi = jnp.arange(BLOCK)[:, None]
    kj = jnp.arange(2 * BLOCK)[None, :]
    dist = qi + BLOCK - kj
    blk = jnp.arange(nb)[:, None, None]
    valid = (dist >= 0) & (dist <= w_s) & (blk * BLOCK + kj - BLOCK >= 0)
    s = jnp.where(valid, s, -jnp.inf)
    m = jnp.max(s, axis=-1, keepdims=True)
    p = jnp.exp(s - m)
    denom = jnp.sum(p, axis=-1)
    o = jnp.einsum('bhrnqk,bhrnkd->bhrnqd', p, vb) / denom[..., None]
    lse = m[..., 0] + jnp.log(denom)
    o = o.reshape(B, H, dilation, Ls, Dh).transpose(0, 1, 3, 2, 4).reshape(B, H, L_pad, Dh)[:, :, :S]
    lse = lse.reshape(B, H, dilation, Ls).transpose(0, 1, 3, 2).reshape(B, H, L_pad)[:, :, :S]
    return o, lse

def dilated_mixture(q, k, v):
    outs, lses = [], []
    for window, dilation in DILATED_PATTERNS:
        o, lse = dilated_branch(q, k, v, window, dilation)
        outs.append(o)
        lses.append(lse)
    o = jnp.stack(outs)
    w = jax.nn.softmax(jnp.stack(lses), axis=0)
    return jnp.sum(w[..., None] * o, axis=0)

def diff_attention(q, k, v, lam):
    B, H, _, S, dd = q.shape
    Dv = v.shape[-1]
    nq = S // BLOCK
    qb = q.reshape(B, H, 2, nq, BLOCK, dd).transpose(3, 0, 1, 2, 4, 5)
    starts = jnp.arange(nq, dtype=jnp.int32) * BLOCK
    kpos = jnp.arange(S, dtype=jnp.int32)

    def attend(args):
        qblk, start = args
        s = jnp.einsum('bhcqd,bhckd->bhcqk', qblk, k,
                       preferred_element_type=jnp.float32) * ATTN_SCALE
        causal = (start + jnp.arange(BLOCK, dtype=jnp.int32))[:, None] >= kpos[None, :]
        p = jax.nn.softmax(jnp.where(causal, s, -jnp.inf), axis=-1)
        a = p[:, :, 0] - lam * p[:, :, 1]
        return jnp.einsum('bhqk,bhkd->bhqd', a, v)

    o = lax.map(attend, (qb, starts))
    return o.transpose(1, 0, 3, 2, 4).reshape(B, S, H, Dv)

def peer_layer(x, w_q, sub_keys, u_table, v_table):
    B, S, D = x.shape
    T = B * S
    tok = x.reshape(T, D)
    q = (tok @ w_q).reshape(T, PEER_HEADS, 2, KEY_DIM)
    s = jnp.einsum('thcd,hckd->thck', q, sub_keys, preferred_element_type=jnp.float32)
    s1, i1 = lax.top_k(s[:, :, 0], PEER_TOPK)
    s2, i2 = lax.top_k(s[:, :, 1], PEER_TOPK)
    cand = (s1[..., :, None] + s2[..., None, :]).reshape(T, PEER_HEADS, PEER_TOPK * PEER_TOPK)
    top, pos = lax.top_k(cand, PEER_TOPK)
    e1 = jnp.take_along_axis(i1, pos // PEER_TOPK, axis=-1)
    e2 = jnp.take_along_axis(i2, pos % PEER_TOPK, axis=-1)
    idx = e1 * N_KEYS + e2
    gates = jax.nn.softmax(top, axis=-1)

    n_chunks = T // TOKEN_CHUNK

    def expert_chunk(args):
        xc, ic, gc = args
        u = u_table[ic]
        act = jax.nn.gelu(jnp.einsum('cd,chkd->chk', xc, u), approximate=False) * gc.astype(xc.dtype)
        v = v_table[ic]
        return jnp.einsum('chk,chkd->cd', act, v)

    out = lax.map(expert_chunk, (tok.reshape(n_chunks, TOKEN_CHUNK, D),
                                 idx.reshape(n_chunks, TOKEN_CHUNK, PEER_HEADS, PEER_TOPK),
                                 gates.reshape(n_chunks, TOKEN_CHUNK, PEER_HEADS, PEER_TOPK)))
    return out.reshape(B, S, D)

def setup_inputs(seed: int = 0) -> dict:
    key = jax.random.key(seed)
    ks = jax.random.split(key, 19)
    f32 = jnp.float32
    L = DEPTH

    def nrm(k, shape, scale):
        return jax.random.normal(k, shape, f32) * scale

    def gain(k, shape):
        return 1.0 + 0.02 * jax.random.normal(k, shape, f32)

    return {
        "x": jax.random.normal(ks[0], (BATCH, SEQ, D_MODEL), f32),
        "attn_norm_g": gain(ks[1], (L, D_MODEL)),
        "w_in": nrm(ks[2], (L, D_MODEL, IN_PROJ_COLS), D_MODEL ** -0.5),
        "q_norm_a": gain(ks[3], (L, HEAD_DIM)),
        "k_norm_a": gain(ks[4], (L, HEAD_DIM)),
        "out_norm_a": gain(ks[5], (L, WIDTH_A)),
        "q_norm_b": gain(ks[6], (L, DIFF_DIM)),
        "k_norm_b": gain(ks[7], (L, DIFF_DIM)),
        "lambda_q1": nrm(ks[8], (L, DIFF_DIM), 0.1),
        "lambda_k1": nrm(ks[9], (L, DIFF_DIM), 0.1),
        "lambda_q2": nrm(ks[10], (L, DIFF_DIM), 0.1),
        "lambda_k2": nrm(ks[11], (L, DIFF_DIM), 0.1),
        "out_norm_b": gain(ks[12], (L, WIDTH_B)),
        "w_out": nrm(ks[13], (L, MIX_WIDTH, D_MODEL), MIX_WIDTH ** -0.5),
        "ffn_norm_g": gain(ks[14], (L, D_MODEL)),
        "w_peer_q": nrm(ks[15], (L, D_MODEL, PEER_HEADS * 2 * KEY_DIM), D_MODEL ** -0.5),
        "peer_sub_keys": nrm(ks[16], (L, PEER_HEADS, 2, N_KEYS, KEY_DIM), KEY_DIM ** -0.5),
        "peer_u": nrm(ks[17], (L, N_EXPERTS, D_MODEL), D_MODEL ** -0.5),
        "peer_v": nrm(ks[18], (L, N_EXPERTS, D_MODEL), (PEER_HEADS * PEER_TOPK) ** -0.5),
    }

def reference(x, attn_norm_g, w_in, q_norm_a, k_norm_a, out_norm_a, q_norm_b, k_norm_b,
              lambda_q1, lambda_k1, lambda_q2, lambda_k2, out_norm_b, w_out,
              ffn_norm_g, w_peer_q, peer_sub_keys, peer_u, peer_v):
    B, S, D = x.shape
    cos, sin = rope_tables(S)
    h = x
    for l in range(DEPTH):
        xn = rms_norm(h, attn_norm_g[l])
        proj = xn @ w_in[l]
        qa, ka, va, qb, kb, vb = jnp.split(
            proj, np.cumsum([WIDTH_A, WIDTH_A, WIDTH_A, WIDTH_B, WIDTH_B])[:].tolist(), axis=-1)

        qa = apply_partial_rope(rms_norm(qa.reshape(B, S, N_HEADS_A, HEAD_DIM), q_norm_a[l]), cos, sin)
        ka = apply_partial_rope(rms_norm(ka.reshape(B, S, N_HEADS_A, HEAD_DIM), k_norm_a[l]), cos, sin)
        va = va.reshape(B, S, N_HEADS_A, HEAD_DIM)
        oa = dilated_mixture(qa.transpose(0, 2, 1, 3), ka.transpose(0, 2, 1, 3), va.transpose(0, 2, 1, 3))
        oa = rms_norm(oa.transpose(0, 2, 1, 3), out_norm_a[l].reshape(N_HEADS_A, HEAD_DIM))
        oa = oa.reshape(B, S, WIDTH_A).astype(x.dtype)

        lam_init = 0.8 - 0.6 * math.exp(-0.3 * l)
        lam = (jnp.exp(jnp.sum(lambda_q1[l].astype(jnp.float32) * lambda_k1[l].astype(jnp.float32)))
               - jnp.exp(jnp.sum(lambda_q2[l].astype(jnp.float32) * lambda_k2[l].astype(jnp.float32)))
               + lam_init)
        qb = apply_partial_rope(rms_norm(qb.reshape(B, S, N_HEADS_B, 2, DIFF_DIM), q_norm_b[l]), cos, sin)
        kb = apply_partial_rope(rms_norm(kb.reshape(B, S, N_HEADS_B, 2, DIFF_DIM), k_norm_b[l]), cos, sin)
        vb = vb.reshape(B, S, N_HEADS_B, DIFF_V_DIM).transpose(0, 2, 1, 3)
        ob = diff_attention(qb.transpose(0, 2, 3, 1, 4), kb.transpose(0, 2, 3, 1, 4), vb, lam)
        ob = rms_norm(ob, out_norm_b[l].reshape(N_HEADS_B, DIFF_V_DIM)) * (1.0 - lam_init)
        ob = ob.reshape(B, S, WIDTH_B).astype(x.dtype)

        h = h + jnp.concatenate([oa, ob], axis=-1) @ w_out[l]

        hn = rms_norm(h, ffn_norm_g[l])
        h = h + peer_layer(hn, w_peer_q[l], peer_sub_keys[l], peer_u[l], peer_v[l]).astype(x.dtype)
    return h.astype(x.dtype)


_drawn_inputs = setup_inputs


def setup_inputs(seed=0):
    import zlib

    import numpy as np

    out = dict(_drawn_inputs(seed))
    spreads = {}
    factors = {'q_norm_a': 4.501,
     'k_norm_a': 5.583,
     'out_norm_a': 16.509,
     'q_norm_b': 5.618,
     'k_norm_b': 6.036,
     'lambda_k1': 8.0,
     'lambda_q2': 8.0,
     'out_norm_b': 21.368,
     'ffn_norm_g': 30.651}
    for name, (base, spread) in spreads.items():
        noise = np.random.default_rng([zlib.crc32(name.encode()), seed]).standard_normal(out[name].shape)
        drawn = base * np.exp(spread * noise) if base else spread * noise
        out[name] = __import__('jax').numpy.asarray(drawn.astype(out[name].dtype))
    for name, factor in factors.items():
        out[name] = (out[name] * factor).astype(out[name].dtype)
    return out
```

```python
import math
from contextlib import ExitStack

import numpy as np
import concourse.bass as bass
from concourse import mybir

F32 = mybir.dt.float32
U32 = mybir.dt.uint32
BF16 = mybir.dt.bfloat16
ALU = mybir.AluOpType
ACT = mybir.ActivationFunctionType
AX_X = mybir.AxisListType.X

P = 128
SEQ, D = 1024, 1024
TILES = SEQ // P
KC = D // P
HD = 64
HEADS_A, HEADS_B = 8, 4
MAPS = HEADS_A + 2 * HEADS_B
PATTERNS = ((128, 1), (512, 4), (2048, 16))
COLS = 512
ROT = HD // 4
HALF = ROT // 2
SCALE = 1.0 / math.sqrt(HD)
EPS = 1e-6
LAM_INIT = 0.8 - 0.6 * math.exp(0.0)
PH, NK, TOPK = 8, 128, 16
PICKS = PH * TOPK
NEG = -1e30
MASK_W = 2 * SEQ - P

S_ONORM, S_OT, S_PROJ, S_HN, S_HNT = range(MAPS, MAPS + 5)
S_HEAD0 = S_HNT + 1
S_IDX = S_HEAD0 + PH
QUAD = 4
SLOTS = 36
PICK0 = SLOTS - PICKS // QUAD
RU = RV = 4
RW = 4
FRONT_STEPS = 114


class Signal:

    def __init__(self, sem, per_tile, unit=1):
        self.sem, self.per_tile, self.unit = sem, per_tile, unit

    def at(self, tile, k):
        return tile * (self.per_tile * self.unit) + k * self.unit


def own_wait(eng, tile):
    if not isinstance(tile, int):
        eng.nop(nofuse=True)


class Steps:

    def __init__(self, eng, signal, tile):
        self.eng, self.counts, self.tile, self.k = eng, signal, tile, 0

    def __call__(self, ins):
        self.k += 1
        ins.then_inc(self.counts.sem, 1)
        self.eng.wait_ge(self.counts.sem, self.counts.at(self.tile, self.k))
        own_wait(self.eng, self.tile)

    def end(self):
        assert self.k == self.counts.per_tile, self.k


def is_first(tile):
    return isinstance(tile, int) and tile == 0


def hybrid_layer(nc, x, attn_norm_g, w_in, q_norm_a, k_norm_a, out_norm_a, q_norm_b, k_norm_b,
                 lambda_q1, lambda_k1, lambda_q2, lambda_k2, out_norm_b, w_out, ffn_norm_g,
                 w_peer_q, peer_sub_keys, peer_u, peer_v, c_ident, c_cos, c_sin, c_mask_a, c_mask_b,
                 c_iota, out):
    ctx = ExitStack()
    with ctx:
        def sb(name, shape, dt=F32):
            return ctx.enter_context(nc.sbuf_tensor(name, shape, dt))

        def sem(name):
            return ctx.enter_context(nc.semaphore(name))

        def signal(name, per_tile, unit=1):
            return Signal(sem(name), per_tile, unit)

        q_dram = nc.dram_tensor("q_scratch", [TILES, P, KC * P], F32, kind="Internal").ap()
        h_dram = nc.dram_tensor("h_scratch", [SEQ, D], F32, kind="Internal").ap()

        ident = sb("ident", [P, P])
        KT = sb("KT", [P, KC, SEQ])
        V = sb("V", [P, TILES, D])
        keysT = sb("keysT", [P, 2 * PH, NK])
        gain_o = sb("gain_o", [P, KC])
        neg_lam = sb("neg_lam", [P, 1])
        arena = sb("arena", [P, 6 * KC * COLS])
        w_in_sb = arena[:, :].rearrange("p (c k n) -> p c k n", c=6, k=KC)
        at = [0]

        def carve(cols):
            at[0] += cols
            assert at[0] <= 6 * KC * COLS
            return arena[:, at[0] - cols:at[0]]

        w_out_sb = carve(KC * D).rearrange("p (k n) -> p k n", k=KC)
        w_ring = carve(RW * KC * P).rearrange("p (r k n) -> p r k n", r=RW, k=KC)
        u_ring = carve(RU * D).rearrange("p (r n) -> p r n", r=RU)
        v_ring = carve(RV * D).rearrange("p (r n) -> p r n", r=RV)
        gain_f = carve(D)
        hn_u = carve(D)
        mask_a = carve(SEQ)
        mask_b = carve(SEQ // 2).bitcast(BF16)
        small = carve(128)
        work = sb("work", [P, 9984])
        qk = work[:, 0:2048].rearrange("p (c n) -> p c n", c=4)
        sq = work[:, 2048:4096].rearrange("p (c n) -> p c n", c=4)
        x_in = work[:, 4096:5120]
        xn = work[:, 5120:6144]
        xnT = work[:, 6144:7168].rearrange("p (k n) -> p k n", k=KC)
        q_stage = work[:, 7168:8192].rearrange("p (k n) -> p k n", k=KC)
        key_raw = work[:, 0:2048].rearrange("p (g n) -> p g n", g=2 * PH)
        cos = work[:, 8192:8256].rearrange("p (t n) -> p t n", t=TILES)
        sin = work[:, 8256:8320].rearrange("p (t n) -> p t n", t=TILES)
        gain_qk = work[:, 8320:8576].rearrange("p (c n) -> p c n", c=4)
        rope = work[:, 8576:9600].rearrange("p (c g n) -> p c g n", c=4, g=32)
        gain_x = work[:, 9600:9608]
        ssq_x = work[:, 9608:9609]
        rms_x = work[:, 9609:9610]
        rms_qk = work[:, 9616:9648]
        lam_in = work[:, 7168:7424].rearrange("p (c n) -> p c n", c=4)
        lam_pr = work[:, 7424:7552].rearrange("p (c n) -> p c n", c=2)
        lam_s = work[:, 9610:9612]

        S = work[:, 0:2048].rearrange("p (b n) -> p b n", b=2)
        turned = work[:, 2048:3072].rearrange("p (k n) -> p k n", k=KC)
        hn = work[:, 3072:4096]
        QT = work[:, 4096:5120].rearrange("p (k n) -> p k n", k=KC)
        y = work[:, 5120:6144]
        diag = work[:, 6144:7168].rearrange("p (b q n) -> p b q n", b=2, q=QUAD)
        qp = work[:, 7168:7680].rearrange("p (b c n) -> p b c n", b=2, c=2)
        cand = work[:, 7680:7936]
        cand2 = work[:, 7936:8192]
        cut = S[:, 0, 0:2 * NK]
        top_c = work[:, 8320:8576].rearrange("p (h c n) -> p h c n", h=PH, c=2)
        top_s = work[:, 8576:8704].rearrange("p (h n) -> p h n", h=PH)
        idx_c = work[:, 8704:8960].bitcast(U32).rearrange("p (h c n) -> p h c n", h=PH, c=2)
        idx_cf = work[:, 2048:2304].rearrange("p (h c n) -> p h c n", h=PH, c=2)
        pos = work[:, 8960:9088].bitcast(U32)
        gate = work[:, 9088:9216]
        dot = work[:, 9216:9344]
        gate_u = work[:, 9344:9472]
        act = work[:, 9472:9600]
        idx_u = work[:, 9600:9728].bitcast(U32)
        idx_v = work[:, 9728:9856].bitcast(U32)
        idx = work[:, 9856:9984].bitcast(U32)
        iota = small[:, 0:16]
        neg_max = small[:, 16:32]
        den = small[:, 32:48]
        inv_den = small[:, 48:64]
        ratio = small[:, 64:68]
        ssq = small[:, 68:80]
        rms = small[:, 80:92]
        ssq_h = small[:, 92:93]
        rms_h = small[:, 93:94]
        gsum = small[:, 96:104]
        hot = work[:, 0:2048].rearrange("p (n j) -> p n j", j=TOPK)
        quot, rem = cand[:, 0:PICKS].bitcast(U32), cand[:, PICKS:2 * PICKS].bitcast(U32)
        part = cand2.rearrange("p (c n) -> p c n", c=2)
        expert = work[:, 8320:8576].rearrange("p (c n) -> p c n", c=2)

        psum = ctx.enter_context(nc.psum_tensor("psum", [P, 8, COLS], F32))
        pS, pO, pAcc, pT = (psum[:, 2 * i:2 * i + 2, :] for i in range(4))
        pT8 = pT.rearrange("p b (k n) -> p (b k) n", n=P)

        ident_in = sem("ident_in")
        consts_in = sem("consts_in")
        w_in_in = [sem(f"w_in_in{c}") for c in range(6)]
        x_loaded = signal("x_loaded", 1, 16)
        q_stored = signal("q_stored", 1, 16)
        consts_b = sem("consts_b")
        w_out_in = sem("w_out_in")
        qt_loaded = signal("qt_loaded", 1, 16)
        x2_loaded = signal("x2_loaded", 1, 16)
        masks_loaded = signal("masks_loaded", 2, 16)
        h_stored = signal("h_stored", 1, 16)
        h_back = signal("h_back", 1, 16)
        y_stored = signal("y_stored", 1, 16)
        w_loaded = [signal(f"w_loaded{r}", 2 * PH // RW, 16) for r in range(RW)]
        u_loaded = [signal(f"u_loaded{r}", PICKS // RU, 16) for r in range(RU)]
        v_loaded = [signal(f"v_loaded{r}", PICKS // RV, 16) for r in range(RV)]
        keys_turned = sem("keys_turned")
        keys_kept = sem("keys_kept")
        lam_step = sem("lam_step")
        lam_exp = sem("lam_exp")
        x_summed = signal("x_summed", 1)
        x_mean = signal("x_mean", 1)
        x_root = signal("x_root", 1)
        x_rms = signal("x_rms", 1)
        xn_ready = signal("xn_ready", 1)
        xn_turned = signal("xn_turned", 1)
        xnT_ready = signal("xnT_ready", 1)
        proj_ready = signal("proj_ready", 6)
        qk_copied = signal("qk_copied", 4)
        v_copied = signal("v_copied", 2)
        qk_step = signal("qk_step", 6)
        qk_mean = signal("qk_mean", 1)
        rotated = signal("rotated", 1)
        qk_root = signal("qk_root", 1)
        k_turned = signal("k_turned", 1)
        k_kept = signal("k_kept", 1)
        q_turned = signal("q_turned", 1)
        q_kept = signal("q_kept", 1)
        s_ready = signal("s_ready", MAPS)
        s_masked = signal("s_masked", MAPS)
        max_step = signal("max_step", MAPS)
        p_ready = signal("p_ready", MAPS)
        mixed = signal("mixed", HEADS_B)
        p_turned = signal("p_turned", HEADS_A + HEADS_B)
        pT_ready = signal("pT_ready", HEADS_A + HEADS_B)
        o_ready = signal("o_ready", HEADS_A + HEADS_B)
        o_read = signal("o_read", 1)
        o_mean = signal("o_mean", 1)
        o_root = signal("o_root", 1)
        o_normed = signal("o_normed", 1)
        o_turned = signal("o_turned", 1)
        oT_ready = signal("oT_ready", 1)
        out_ready = signal("out_ready", 1)
        h_ready = signal("h_ready", 1)
        h_summed = signal("h_summed", 1)
        h_mean = signal("h_mean", 1)
        h_root = signal("h_root", 1)
        hn_ready = signal("hn_ready", 1)
        hn_turned = signal("hn_turned", 1)
        hnT_ready = signal("hnT_ready", 1)
        qp_ready = signal("qp_ready", PH)
        qp_kept = signal("qp_kept", PH)
        sc_ready = signal("sc_ready", PH)
        selected = signal("selected", PH)
        idx_ready = signal("idx_ready", 1)
        gate_shifted = signal("gate_shifted", 1)
        front_step = signal("front_step", FRONT_STEPS)
        gate_exp = signal("gate_exp", 1)
        u_used = signal("u_used", PICKS)
        gelu_done = signal("gelu_done", 1)
        act_ready = signal("act_ready", 1)
        handed = signal("handed", 2)
        diag_ready = signal("diag_ready", PICKS // QUAD)
        v_used = signal("v_used", PICKS)
        idx_u_set = signal("idx_u_set", 1)
        idx_v_set = signal("idx_v_set", 1)
        y_ready = signal("y_ready", 1)

        block = ctx.enter_context(nc.Block())

        def iterations(eng, body):
            body(0, None, None)
            body(1, 0, None)
            body(2, 1, 0)
            with eng.Fori(3, TILES) as j:
                body(j, j - 1, j - 2)
            body(None, TILES - 1, TILES - 2)
            body(None, None, TILES - 1)

        def first_phase(eng, body):
            body(0, False)
            with eng.Fori(1, TILES - 1) as t:
                body(t, False)
            body(TILES - 1, True)

        def rows(ap, t):
            return ap[bass.ds(t * P, P), :]

        def col(vec, k):
            return vec.rearrange("(k p) -> p k", k=k)

        CONSTS_A = 12
        CONSTS_B = 2
        ORDER = (0, 1, 3, 4, 2, 5)

        @block.sync
        def _(sp):
            row = lambda v: v.rearrange("(a n) -> a n", a=1)
            sp.dma_start(x_in, x[0:P, :]).then_inc(x_loaded.sem, 16)
            sp.dma_start(ident[:, :], c_ident).then_inc(ident_in, 16)
            sp.dma_start(gain_x, col(attn_norm_g, KC), allow_slow_non_contiguous=True).then_inc(ident_in, 16)
            sp.dma_start(key_raw, peer_sub_keys.rearrange("h c k d -> k (h c) d")).then_inc(ident_in, 16)
            for c in ORDER:
                sp.dma_start(w_in_sb[:, c], w_in[:, c * COLS:(c + 1) * COLS].rearrange("(k p) n -> p k n", p=P))\
                  .then_inc(w_in_in[c], 16)
                if c == 0:
                    sp.dma_start(cos, c_cos.rearrange("(t p) n -> p t n", p=P)).then_inc(consts_in, 16)
                    sp.dma_start(sin, c_sin.rearrange("(t p) n -> p t n", p=P)).then_inc(consts_in, 16)
                    sp.dma_start(gain_o[:, 0:KC // 2], col(out_norm_a, KC // 2), allow_slow_non_contiguous=True).then_inc(consts_in, 16)
                    sp.dma_start(gain_o[:, KC // 2:KC], col(out_norm_b, KC // 2), allow_slow_non_contiguous=True).then_inc(consts_in, 16)
                    for n, g in enumerate((q_norm_a, k_norm_a, q_norm_b, k_norm_b)):
                        sp.dma_start(gain_qk[:, n, :], row(g).to_broadcast((P, HD))).then_inc(consts_in, 16)
                    for n, v in enumerate((lambda_q1, lambda_q2, lambda_k1, lambda_k2)):
                        sp.dma_start(lam_in[:, n, :], row(v).to_broadcast((P, HD))).then_inc(consts_in, 16)

            def body(t, last):
                if not last:
                    sp.wait_ge(xn_ready.sem, xn_ready.at(t, 1))
                    own_wait(sp, t)
                    sp.dma_start(x_in, rows(x, t + 1)).then_inc(x_loaded.sem, 16)
                sp.wait_ge(q_kept.sem, q_kept.at(t, 1))
                own_wait(sp, t)
                sp.dma_start(q_dram[bass.ds(t, 1)].rearrange("a p n -> (a p) n"), q_stage).then_inc(q_stored.sem, 16)
            first_phase(sp, body)

            sp.wait_ge(proj_ready.sem, proj_ready.at(TILES - 1, 6))
            sp.wait_ge(q_kept.sem, q_kept.at(TILES - 1, 1))
            sp.wait_ge(k_kept.sem, k_kept.at(TILES - 1, 1))
            sp.dma_start(iota, c_iota).then_inc(consts_b, 16)
            sp.dma_start(gain_f, row(ffn_norm_g).to_broadcast((P, D))).then_inc(consts_b, 16)
            sp.wait_ge(q_stored.sem, q_stored.at(TILES - 1, 1))

            def load_w(t, n):
                if n >= RW:
                    sp.wait_ge(qp_ready.sem, qp_ready.at(t, (n - RW) // 2 + 1))
                    own_wait(sp, t)
                elif not is_first(t):
                    sp.wait_ge(qp_ready.sem, qp_ready.at(t - 1, PH))
                    own_wait(sp, t)
                sp.dma_start(w_ring[:, n % RW], w_peer_q[:, n * P:(n + 1) * P].rearrange("(k p) n -> p k n", p=P))\
                  .then_inc(w_loaded[n % RW].sem, 16)

            def body(tf, tu, tv):
                if tf is not None:
                    if not is_first(tf):
                        sp.wait_ge(s_ready.sem, s_ready.at(tf - 1, MAPS))
                        own_wait(sp, tf)
                        sp.wait_ge(handed.sem, handed.at(tf - 1, 1))
                        own_wait(sp, tf)
                    sp.dma_start(QT, q_dram[bass.ds(tf, 1)].rearrange("a p n -> (a p) n")).then_inc(qt_loaded.sem, 16)
                    sp.dma_start(hn, rows(x, tf)).then_inc(x2_loaded.sem, 16)
                    if not is_first(tf):
                        sp.wait_ge(s_masked.sem, s_masked.at(tf - 1, MAPS))
                        own_wait(sp, tf)
                    window = bass.ds((TILES - 1 - tf) * P, SEQ)
                    sp.dma_start(mask_a, c_mask_a[:, window]).then_inc(masks_loaded.sem, 16)
                    sp.dma_start(mask_b, c_mask_b[:, window]).then_inc(masks_loaded.sem, 16)
                    if is_first(tf):
                        sp.dma_start(w_out_sb, w_out.rearrange("(k p) n -> p k n", p=P)).then_inc(w_out_in, 16)
                    for n in range(RW):
                        load_w(tf, n)
                    sp.wait_ge(h_ready.sem, h_ready.at(tf, 1))
                    own_wait(sp, tf)
                    sp.dma_start(rows(h_dram, tf), hn).then_inc(h_stored.sem, 16)
                    for n in range(RW, 2 * PH):
                        load_w(tf, n)
                if tv is not None:
                    if not is_first(tv):
                        sp.wait_ge(y_stored.sem, y_stored.at(tv - 1, 1))
                        own_wait(sp, tv)
                    sp.wait_ge(h_stored.sem, h_stored.at(tv, 1))
                    own_wait(sp, tv)
                    sp.dma_start(y, rows(h_dram, tv)).then_inc(h_back.sem, 16)
                    sp.wait_ge(y_ready.sem, y_ready.at(tv, 1))
                    own_wait(sp, tv)
                    sp.dma_start(rows(out, tv), y).then_inc(y_stored.sem, 16)
            iterations(sp, body)
            sp.wait_ge(y_stored.sem, y_stored.at(TILES - 1, 1))

        @block.gpsimd
        def _(pool):
            def gather(ring, r, table, idx_tile, p, loaded):
                nc.gpsimd.indirect_dma_start(
                    out=ring[:, r, :], out_offset=None, in_=table,
                    in_offset=bass.IndirectOffsetOnAxis(ap=idx_tile[:, p:p + 1], axis=0)).then_inc(loaded.sem, 16)

            def body(tf, tu, tv):
                for p in range(PICKS):
                    if tv is not None:
                        if p >= RV:
                            pool.wait_ge(v_used.sem, v_used.at(tv, p - RV + 1))
                        elif not is_first(tv):
                            pool.wait_ge(v_used.sem, v_used.at(tv - 1, PICKS - RV + 1 + p))
                        own_wait(pool, tv)
                        gather(v_ring, p % RV, peer_v, idx_v, p, v_loaded[p % RV])
                    if tu is not None:
                        if p >= RU:
                            pool.wait_ge(u_used.sem, u_used.at(tu, p - RU + 1))
                        elif not is_first(tu):
                            pool.wait_ge(u_used.sem, u_used.at(tu - 1, PICKS - RU + 1 + p))
                        own_wait(pool, tu)
                        gather(u_ring, p % RU, peer_u, idx_u, p, u_loaded[p % RU])
                if tu is not None:
                    if tv is not None:
                        for r in range(RV):
                            pool.wait_ge(v_loaded[r].sem, v_loaded[r].at(tv, PICKS // RV))
                    for r in range(RU):
                        pool.wait_ge(u_loaded[r].sem, u_loaded[r].at(tu, PICKS // RU))
                    own_wait(pool, tu)
                    nc.gpsimd.tensor_copy(idx_v, idx_u).then_inc(idx_v_set.sem, 1)
                    pool.wait_ge(idx_v_set.sem, idx_v_set.at(tu, 1))
                if tf is not None:
                    pool.wait_ge(idx_ready.sem, idx_ready.at(tf, 1))
                    own_wait(pool, tf)
                    nc.gpsimd.tensor_copy(idx_u, idx).then_inc(idx_u_set.sem, 1)
                    pool.wait_ge(idx_u_set.sem, idx_u_set.at(tf, 1))
            iterations(pool, body)

        @block.tensor
        def _(pe):
            def turn_x(t):
                pe.wait_ge(xn_ready.sem, xn_ready.at(t, 1))
                for k in range(KC):
                    last = nc.tensor.transpose(pT8[:, k, :], xn[:, k * P:(k + 1) * P], ident[:, :])
                last.then_inc(xn_turned.sem, 1)

            def project(t, n, cold):
                c = ORDER[n]
                if cold:
                    pe.wait_ge(w_in_in[c], 16)
                if not is_first(t):
                    if n < 4:
                        pe.wait_ge(qk_copied.sem, qk_copied.at(t - 1, n + 1))
                    else:
                        pe.wait_ge(v_copied.sem, v_copied.at(t - 1, n - 3))
                for k in range(KC):
                    last = nc.tensor.matmul(psum[:, n, :], xnT[:, k, :], w_in_sb[:, c, k, :],
                                            start=(k == 0), stop=(k == KC - 1))
                last.then_inc(proj_ready.sem, 1)

            def body(t, last_tile):
                pe.wait_ge(xnT_ready.sem, xnT_ready.at(t, 1))
                for n in range(4):
                    project(t, n, is_first(t))
                if not is_first(t):
                    pe.wait_ge(q_kept.sem, q_kept.at(t - 1, 1))
                if not last_tile:
                    turn_x(t + 1)
                for n in range(4, 6):
                    project(t, n, is_first(t))
                if not last_tile:
                    pe.wait_ge(xnT_ready.sem, xnT_ready.at(t + 1, 1))
                pe.wait_ge(rotated.sem, rotated.at(t, 1))
                for g in range(KC):
                    last = nc.tensor.transpose(pT8[:, g, :], qk[:, 1 + 2 * (g // 4), (g % 4) * P:(g % 4 + 1) * P],
                                               ident[:, :])
                last.then_inc(k_turned.sem, 1)
                pe.wait_ge(k_kept.sem, k_kept.at(t, 1))
                for g in range(KC):
                    last = nc.tensor.transpose(pT8[:, g, :], qk[:, 2 * (g // 4), (g % 4) * P:(g % 4 + 1) * P],
                                               ident[:, :])
                last.then_inc(q_turned.sem, 1)

            pe.wait_ge(ident_in, 48)
            turn_x(0)
            pe.wait_ge(xnT_ready.sem, xnT_ready.at(0, 1))
            for half in range(2):
                if half:
                    pe.wait_ge(keys_kept, half)
                for g in range(PH):
                    last = nc.tensor.transpose(pT8[:, g, :], key_raw[:, half * PH + g, :], ident[:, :])
                last.then_inc(keys_turned, 1)
            pe.wait_ge(keys_kept, 2)
            first_phase(pe, body)

            def heads_slice(m):
                pair, side = (m // 2, m % 2)
                return pair, slice(side * HD, (side + 1) * HD)

            def scores(t, m):
                if m == 0:
                    pe.wait_ge(qt_loaded.sem, qt_loaded.at(t, 1))
                    if is_first(t):
                        pe.wait_ge(v_copied.sem, v_copied.at(TILES - 1, 2))
                        pe.wait_ge(qk_copied.sem, qk_copied.at(TILES - 1, 4))
                        pe.wait_ge(k_kept.sem, k_kept.at(TILES - 1, 1))
                        pe.wait_ge(q_kept.sem, q_kept.at(TILES - 1, 1))
                    else:
                        pe.wait_ge(selected.sem, selected.at(t - 1, PH))
                else:
                    pe.wait_ge(s_masked.sem, s_masked.at(t, m))
                pair, rows_ = heads_slice(m)
                for n in range(2):
                    last = nc.tensor.matmul(pS[:, n, :], QT[rows_, pair, :], KT[rows_, pair, n * COLS:(n + 1) * COLS],
                                            start=True, stop=True)
                last.then_inc(s_ready.sem, 1)

            def turn_p(t, a, src, ready):
                pe.wait_ge(*ready)
                if a == 0:
                    if not is_first(t):
                        pe.wait_ge(qp_kept.sem, qp_kept.at(t - 1, PH))
                else:
                    pe.wait_ge(pT_ready.sem, pT_ready.at(t, a))
                for k in range(KC):
                    last = nc.tensor.transpose(pT8[:, k, :], src[:, k * P:(k + 1) * P], ident[:, :])
                last.then_inc(p_turned.sem, 1)

            def times_v(t, a):
                pe.wait_ge(pT_ready.sem, pT_ready.at(t, a + 1))
                if a == 0 and not is_first(t):
                    pe.wait_ge(o_read.sem, o_read.at(t - 1, 1))
                if a < HEADS_A:
                    dst, c0, w = pO[:, 0, a * HD:(a + 1) * HD], a * HD, HD
                else:
                    b = a - HEADS_A
                    dst, c0, w = pO[:, 1, b * P:(b + 1) * P], COLS + b * P, P
                for k in range(KC):
                    last = nc.tensor.matmul(dst, turned[:, k, :], V[:, k, c0:c0 + w], start=(k == 0), stop=(k == KC - 1))
                last.then_inc(o_ready.sem, 1)

            def turn_o(t):
                pe.wait_ge(o_normed.sem, o_normed.at(t, 1))
                for k in range(KC):
                    last = nc.tensor.transpose(pT8[:, k, :], S[:, 0, k * P:(k + 1) * P], ident[:, :])
                last.then_inc(o_turned.sem, 1)

            def out_proj(t):
                pe.wait_ge(oT_ready.sem, oT_ready.at(t, 1))
                if is_first(t):
                    pe.wait_ge(w_out_in, 16)
                for k in range(KC):
                    for n in range(2):
                        last = nc.tensor.matmul(pS[:, n, :], turned[:, k, :], w_out_sb[:, k, n * COLS:(n + 1) * COLS],
                                                start=(k == 0), stop=(k == KC - 1))
                last.then_inc(out_ready.sem, 1)

            def turn_hn(t):
                pe.wait_ge(hn_ready.sem, hn_ready.at(t, 1))
                for k in range(KC):
                    last = nc.tensor.transpose(pT8[:, k, :], hn[:, k * P:(k + 1) * P], ident[:, :])
                last.then_inc(hn_turned.sem, 1)

            def expert_query(t, h):
                if h == 0:
                    pe.wait_ge(hnT_ready.sem, hnT_ready.at(t, 1))
                if h >= 2:
                    pe.wait_ge(qp_kept.sem, qp_kept.at(t, h - 1))
                for c in range(2):
                    n = 2 * h + c
                    pe.wait_ge(w_loaded[n % RW].sem, w_loaded[n % RW].at(t, n // RW + 1))
                    for k in range(KC):
                        last = nc.tensor.matmul(pT[:, h % 2, c * P:(c + 1) * P], w_ring[:, n % RW, k, :],
                                                turned[:, k, :], start=(k == 0), stop=(k == KC - 1))
                last.then_inc(qp_ready.sem, 1)

            def key_scores(t, h):
                pe.wait_ge(qp_kept.sem, qp_kept.at(t, h + 1))
                if h == 0:
                    pe.wait_ge(h_ready.sem, h_ready.at(t, 1))
                if h >= 2:
                    pe.wait_ge(selected.sem, selected.at(t, h - 1))
                for c in range(2):
                    last = nc.tensor.matmul(pS[:, h % 2, c * P:(c + 1) * P], qp[:, h % 2, c, :],
                                            keysT[:, 2 * h + c, :], start=True, stop=True)
                last.then_inc(sc_ready.sem, 1)

            def front(t, s, third):
                if s < MAPS:
                    if third == 0:
                        scores(t, s)
                    if s < HEADS_A:
                        if third == 1:
                            turn_p(t, s, S[:, s % 2, :], (p_ready.sem, p_ready.at(t, s + 1)))
                        if third == 2:
                            times_v(t, s)
                    elif s % 2:
                        b = (s - HEADS_A) // 2
                        if third == 1:
                            turn_p(t, HEADS_A + b, S[:, 0, :], (mixed.sem, mixed.at(t, b + 1)))
                        if third == 2:
                            times_v(t, HEADS_A + b)
                elif s == S_OT and third == 0:
                    turn_o(t)
                elif s == S_PROJ and third == 0:
                    out_proj(t)
                elif s == S_HNT and third == 0:
                    turn_hn(t)
                elif S_HEAD0 <= s < S_IDX:
                    if third == 0:
                        expert_query(t, s - S_HEAD0)
                    if third == 1:
                        key_scores(t, s - S_HEAD0)

            def add_row(t, p):
                pe.wait_ge(v_loaded[p % RV].sem, v_loaded[p % RV].at(t, p // RV + 1))
                if p % QUAD == 0:
                    pe.wait_ge(diag_ready.sem, diag_ready.at(t, p // QUAD + 1))
                if p == 0 and not is_first(t):
                    pe.wait_ge(y_ready.sem, y_ready.at(t - 1, 1))
                for n in range(2):
                    last = nc.tensor.matmul(pAcc[:, n, :], diag[:, (p // QUAD) % 2, p % QUAD, :],
                                            v_ring[:, p % RV, n * COLS:(n + 1) * COLS],
                                            start=(p == 0), stop=(p == PICKS - 1))
                last.then_inc(v_used.sem, 1)

            def body(tf, tu, tv):
                for s in range(SLOTS):
                    for third in range(3):
                        if tf is not None:
                            front(tf, s, third)
                        if tv is not None and s >= PICK0 and third < 2:
                            p = (s - PICK0) * QUAD + 2 * third
                            add_row(tv, p)
                            add_row(tv, p + 1)
            iterations(pe, body)

        @block.scalar
        def _(act_e):
            e = act_e

            def norm_x(t):
                e.wait_ge(x_loaded.sem, x_loaded.at(t, 1))
                if not is_first(t):
                    e.wait_ge(xn_turned.sem, xn_turned.at(t - 1, 1))
                e.activation(xn, x_in, ACT.Square, accum_out=ssq_x).then_inc(x_summed.sem, 1)
                e.wait_ge(x_mean.sem, x_mean.at(t, 1))
                e.activation(rms_x, ssq_x, ACT.Sqrt).then_inc(x_root.sem, 1)
                e.wait_ge(x_rms.sem, x_rms.at(t, 1))
                e.activation(xn, x_in, ACT.Copy, scale=rms_x).then_inc(xn_ready.sem, 1)

            def body(t, last):
                if not last:
                    norm_x(t + 1)
                for n in range(4):
                    e.wait_ge(proj_ready.sem, proj_ready.at(t, n + 1))
                    if is_first(t):
                        if n == 0:
                            e.wait_ge(keys_kept, 2)
                    elif n == 0:
                        e.wait_ge(q_turned.sem, q_turned.at(t - 1, 1))
                    e.activation(qk[:, n, :], psum[:, n, :], ACT.Copy).then_inc(qk_copied.sem, 1)
                e.wait_ge(qk_mean.sem, qk_mean.at(t, 1))
                e.activation(rms_qk, rms_qk, ACT.Sqrt).then_inc(qk_root.sem, 1)
                for n in range(2):
                    e.wait_ge(proj_ready.sem, proj_ready.at(t, n + 5))
                    e.activation(V[:, bass.ds(t, 1), n * COLS:(n + 1) * COLS].rearrange("p a n -> p (a n)"),
                                 psum[:, 4 + n, :], ACT.Copy).then_inc(v_copied.sem, 1)
                e.wait_ge(k_turned.sem, k_turned.at(t, 1))
                e.activation(KT[:, :, bass.ds(t * P, P)], pT8, ACT.Copy).then_inc(k_kept.sem, 1)
            norm_x(0)
            for half in range(2):
                e.wait_ge(keys_turned, half + 1)
                e.activation(keysT[:, half * PH:(half + 1) * PH, :], pT8, ACT.Copy).then_inc(keys_kept, 1)
            e.wait_ge(lam_step, 2)
            e.activation(lam_s, lam_s, ACT.Exp).then_inc(lam_exp, 1)
            first_phase(e, body)

            def front(t, s):
                if s < MAPS:
                    e.wait_ge(max_step.sem, max_step.at(t, s + 1))
                    if s == 0 and not is_first(t):
                        e.wait_ge(o_read.sem, o_read.at(t - 1, 1))
                    e.activation(S[:, s % 2, :], S[:, s % 2, :], ACT.Exp, bias=neg_max[:, s:s + 1], scale=SCALE,
                                 accum_out=den[:, s:s + 1]).then_inc(p_ready.sem, 1)
                    if s < HEADS_A or s % 2:
                        a = s if s < HEADS_A else HEADS_A + (s - HEADS_A) // 2
                        e.wait_ge(p_turned.sem, p_turned.at(t, a + 1))
                        if a:
                            e.wait_ge(o_ready.sem, o_ready.at(t, a))
                        elif not is_first(t):
                            e.wait_ge(qp_ready.sem, qp_ready.at(t - 1, PH))
                        e.activation(turned, pT8, ACT.Copy).then_inc(pT_ready.sem, 1)
                elif s == S_ONORM:
                    e.wait_ge(o_mean.sem, o_mean.at(t, 1))
                    e.activation(rms, ssq, ACT.Sqrt).then_inc(o_root.sem, 1)
                elif s == S_HN:
                    e.wait_ge(h_ready.sem, h_ready.at(t, 1))
                    e.activation(S[:, 1, :], hn, ACT.Square, accum_out=ssq_h).then_inc(h_summed.sem, 1)
                    e.wait_ge(h_mean.sem, h_mean.at(t, 1))
                    e.activation(rms_h, ssq_h, ACT.Sqrt).then_inc(h_root.sem, 1)
                elif s == S_HNT:
                    e.wait_ge(hn_turned.sem, hn_turned.at(t, 1))
                    e.wait_ge(out_ready.sem, out_ready.at(t, 1))
                    e.activation(turned, pT8, ACT.Copy).then_inc(hnT_ready.sem, 1)
                elif S_HEAD0 <= s < S_IDX:
                    h = s - S_HEAD0
                    e.wait_ge(qp_ready.sem, qp_ready.at(t, h + 1))
                    if h >= 2:
                        e.wait_ge(sc_ready.sem, sc_ready.at(t, h - 1))
                    e.activation(qp[:, h % 2], pT[:, h % 2, 0:2 * P].rearrange("p (c n) -> p c n", c=2), ACT.Copy)\
                     .then_inc(qp_kept.sem, 1)
                elif s == S_IDX:
                    e.wait_ge(gate_shifted.sem, gate_shifted.at(t, 1))
                    e.activation(gate, gate, ACT.Exp).then_inc(gate_exp.sem, 1)

            def body(tf, tu, tv):
                if tf is not None:
                    for s in range(SLOTS):
                        front(tf, s)
                if tu is not None:
                    e.wait_ge(u_used.sem, u_used.at(tu, PICKS))
                    e.activation(dot, dot, ACT.Gelu).then_inc(gelu_done.sem, 1)
            iterations(e, body)

        @block.vector
        def _(dve):
            v = nc.vector

            def norm_x(t):
                dve.wait_ge(x_summed.sem, x_summed.at(t, 1))
                v.tensor_scalar(ssq_x, ssq_x, 1.0 / D, EPS, ALU.mult, ALU.add).then_inc(x_mean.sem, 1)
                dve.wait_ge(x_root.sem, x_root.at(t, 1))
                v.reciprocal(rms_x, rms_x).then_inc(x_rms.sem, 1)

            def keep_xT(t):
                dve.wait_ge(xn_turned.sem, xn_turned.at(t, 1))
                if not is_first(t):
                    dve.wait_ge(proj_ready.sem, proj_ready.at(t - 1, 6))
                v.tensor_tensor(xnT, pT8, gain_x.unsqueeze(2).to_broadcast((P, KC, P)), ALU.mult)\
                 .then_inc(xnT_ready.sem, 1)

            def body(t, last):
                if not last:
                    norm_x(t + 1)
                groups = qk.rearrange("p c (g n) -> p (c g) n", n=HD)
                sq_g = sq.rearrange("p c (g n) -> p (c g) n", n=HD)
                dve.wait_ge(qk_copied.sem, qk_copied.at(t, 4))
                st = Steps(dve, qk_step, t)
                st(v.tensor_tensor(sq, qk, qk, ALU.mult))
                st(v.tensor_reduce(rms_qk, sq_g, AX_X, ALU.add))
                v.tensor_scalar(rms_qk, rms_qk, 1.0 / HD, EPS, ALU.mult, ALU.add).then_inc(qk_mean.sem, 1)
                dve.wait_ge(qk_root.sem, qk_root.at(t, 1))
                st(v.reciprocal(rms_qk, rms_qk))
                st(v.tensor_tensor(groups, groups, rms_qk.unsqueeze(2).to_broadcast((P, 32, HD)), ALU.mult))
                for c in range(4):
                    g = qk[:, c, :].rearrange("p (g n) -> p g n", n=HD)
                    ins = v.tensor_tensor(g, g, gain_qk[:, c:c + 1, :].to_broadcast((P, 8, HD)), ALU.mult)
                st(ins)
                x1, x2 = groups[:, :, 0:HALF], groups[:, :, HALF:ROT]
                ct = cos[:, bass.ds(t, 1), :].to_broadcast((P, 32, HALF))
                si = sin[:, bass.ds(t, 1), :].to_broadcast((P, 32, HALF))
                v.tensor_tensor(rope[:, 0], x1, ct, ALU.mult)
                v.tensor_tensor(rope[:, 1], x2, si, ALU.mult)
                v.tensor_tensor(rope[:, 2], x2, ct, ALU.mult)
                st(v.tensor_tensor(rope[:, 3], x1, si, ALU.mult))
                v.tensor_tensor(x1, rope[:, 0], rope[:, 1], ALU.subtract)
                v.tensor_tensor(x2, rope[:, 2], rope[:, 3], ALU.add).then_inc(rotated.sem, 1)
                st.end()
                if not last:
                    keep_xT(t + 1)
                dve.wait_ge(q_turned.sem, q_turned.at(t, 1))
                if not is_first(t):
                    dve.wait_ge(q_stored.sem, q_stored.at(t - 1, 1))
                v.tensor_copy(q_stage, pT8).then_inc(q_kept.sem, 1)

            norm_x(0)
            keep_xT(0)
            dve.wait_ge(consts_in, 16 * CONSTS_A)
            v.tensor_tensor(lam_pr, lam_in[:, 0:2, :], lam_in[:, 2:4, :], ALU.mult).then_inc(lam_step, 1)
            dve.wait_ge(lam_step, 1)
            v.tensor_reduce(lam_s, lam_pr, AX_X, ALU.add).then_inc(lam_step, 1)
            dve.wait_ge(lam_exp, 1)
            v.tensor_tensor(neg_lam[:, :], lam_s[:, 1:2], lam_s[:, 0:1], ALU.subtract).then_inc(lam_step, 1)
            dve.wait_ge(lam_step, 3)
            v.tensor_scalar(neg_lam[:, :], neg_lam[:, :], -LAM_INIT, None, ALU.add).then_inc(lam_step, 1)
            dve.wait_ge(lam_step, 4)
            first_phase(dve, body)

            def attention(t, m):
                dve.wait_ge(s_ready.sem, s_ready.at(t, m + 1))
                if m == 0:
                    if is_first(t):
                        dve.wait_ge(consts_b, 16 * CONSTS_B)
                    dve.wait_ge(masks_loaded.sem, masks_loaded.at(t, 2))
                if 2 <= m <= HEADS_A + 1:
                    dve.wait_ge(p_turned.sem, p_turned.at(t, m - 1))
                elif m > HEADS_A and m % 2 == 0:
                    dve.wait_ge(p_turned.sem, p_turned.at(t, HEADS_A + (m - HEADS_A) // 2))
                own_wait(dve, t)
                v.tensor_tensor_reduce(
                    out=S[:, m % 2, :], in0=pS.rearrange("p b n -> p (b n)"), in1=mask_a if m < HEADS_A else mask_b, scale=1.0,
                    scalar=3.0 * NEG, op0=ALU.add, op1=ALU.max, accum_out=neg_max[:, m:m + 1]).then_inc(s_masked.sem, 1)
                dve.wait_ge(s_masked.sem, s_masked.at(t, m + 1))
                v.tensor_scalar(neg_max[:, m:m + 1], neg_max[:, m:m + 1], -SCALE, None, ALU.mult).then_inc(max_step.sem, 1)

            def mix(t, b, st):
                m = HEADS_A + 2 * b
                dve.wait_ge(p_ready.sem, p_ready.at(t, m + 2))
                st(v.reciprocal(ratio[:, b:b + 1], den[:, m + 1:m + 2]))
                st(v.scalar_tensor_tensor(ratio[:, b:b + 1], den[:, m:m + 1], neg_lam[:, :], ratio[:, b:b + 1],
                                          ALU.mult, ALU.mult))
                v.scalar_tensor_tensor(S[:, 0, :], S[:, 1, :], ratio[:, b:b + 1], S[:, 0, :],
                                       ALU.mult, ALU.add).then_inc(mixed.sem, 1)

            def norm_o(t, st):
                O, O2 = S[:, 0, :], S[:, 1, :]
                a = lambda z: z[:, 0:COLS].rearrange("p (h n) -> p h n", n=HD)
                b = lambda z: z[:, COLS:D].rearrange("p (h n) -> p h n", n=P)
                wide = lambda z, n: z.unsqueeze(2).to_broadcast((P, z.shape[1], n))
                dve.wait_ge(o_ready.sem, o_ready.at(t, HEADS_A + HEADS_B))
                v.reciprocal(inv_den[:, 0:HEADS_A], den[:, 0:HEADS_A])
                st(v.reciprocal(inv_den[:, HEADS_A:HEADS_A + HEADS_B], den[:, HEADS_A:MAPS:2]))
                v.tensor_tensor(a(O), pO[:, 0, :].rearrange("p (h n) -> p h n", n=HD),
                                wide(inv_den[:, 0:HEADS_A], HD), ALU.mult)
                v.tensor_tensor(b(O), pO[:, 1, :].rearrange("p (h n) -> p h n", n=P),
                                wide(inv_den[:, HEADS_A:HEADS_A + HEADS_B], P), ALU.mult).then_inc(o_read.sem, 1)
                dve.wait_ge(o_read.sem, o_read.at(t, 1))
                st(v.tensor_tensor(O2, O, O, ALU.mult))
                v.tensor_reduce(ssq[:, 0:HEADS_A], a(O2), AX_X, ALU.add)
                st(v.tensor_reduce(ssq[:, HEADS_A:], b(O2), AX_X, ALU.add))
                v.tensor_scalar(ssq[:, 0:HEADS_A], ssq[:, 0:HEADS_A], 1.0 / HD, EPS, ALU.mult, ALU.add)
                v.tensor_scalar(ssq[:, HEADS_A:], ssq[:, HEADS_A:], 1.0 / P, EPS, ALU.mult, ALU.add)\
                 .then_inc(o_mean.sem, 1)
                dve.wait_ge(o_root.sem, o_root.at(t, 1))
                st(v.reciprocal(rms, rms))
                st(v.tensor_scalar(rms[:, HEADS_A:], rms[:, HEADS_A:], 1.0 - LAM_INIT, None, ALU.mult))
                v.tensor_tensor(a(O), a(O), wide(rms[:, 0:HEADS_A], HD), ALU.mult)
                v.tensor_tensor(b(O), b(O), wide(rms[:, HEADS_A:], P), ALU.mult).then_inc(o_normed.sem, 1)

            def keep_oT(t):
                dve.wait_ge(o_turned.sem, o_turned.at(t, 1))
                v.tensor_tensor(turned, pT8, gain_o[:, :].unsqueeze(2).to_broadcast((P, KC, P)), ALU.mult)\
                 .then_inc(oT_ready.sem, 1)

            def residual(t):
                dve.wait_ge(out_ready.sem, out_ready.at(t, 1))
                dve.wait_ge(x2_loaded.sem, x2_loaded.at(t, 1))
                v.tensor_tensor(hn, pS.rearrange("p b n -> p (b n)"), hn, ALU.add).then_inc(h_ready.sem, 1)

            def norm_h(t, st):
                dve.wait_ge(h_summed.sem, h_summed.at(t, 1))
                v.tensor_scalar(ssq_h, ssq_h, 1.0 / D, EPS, ALU.mult, ALU.add).then_inc(h_mean.sem, 1)
                dve.wait_ge(h_root.sem, h_root.at(t, 1))
                st(v.reciprocal(rms_h, rms_h))
                dve.wait_ge(h_stored.sem, h_stored.at(t, 1))
                v.scalar_tensor_tensor(hn, hn, rms_h, gain_f, ALU.mult, ALU.mult).then_inc(hn_ready.sem, 1)

            def select(t, h, st):
                def top16(values, spare, best, where, last):
                    st(v.max(best[:, 0:8], values))
                    v.max_index(where[:, 0:8], best[:, 0:8], values)
                    st(v.match_replace(spare, best[:, 0:8], values, 3.0 * NEG))
                    st(v.max(best[:, 8:16], spare))
                    return v.max_index(where[:, 8:16], best[:, 8:16], spare)

                dve.wait_ge(sc_ready.sem, sc_ready.at(t, h + 1))
                own_wait(dve, t)
                for c in range(2):
                    last = top16(pS[:, h % 2, c * P:(c + 1) * P], cut[:, c * P:(c + 1) * P],
                                 top_c[:, h, c, :], idx_c[:, h, c, :], False)
                last.then_inc(selected.sem, 1)
                pairs = cand.rearrange("p (i j) -> p i j", i=TOPK)
                st(v.tensor_tensor(pairs, top_c[:, h, 0, :].unsqueeze(2).to_broadcast((P, TOPK, TOPK)),
                                   top_c[:, h, 1:2, :].to_broadcast((P, TOPK, TOPK)), ALU.add))
                st(top16(cand, cand2, top_s[:, h, :], pos[:, h * TOPK:(h + 1) * TOPK], True))

            def experts(t, st):
                v.tensor_scalar(quot, pos, 4, None, ALU.logical_shift_right)
                v.tensor_scalar(rem, pos, TOPK - 1, None, ALU.bitwise_and)
                st(v.tensor_copy(idx_cf, idx_c))
                v.tensor_copy(part[:, 0], quot)
                st(v.tensor_copy(part[:, 1], rem))
                hot4 = hot.rearrange("p (h n) j -> p h n j", h=PH)
                for c in range(2):
                    st(v.tensor_tensor(hot, part[:, c].unsqueeze(2).to_broadcast((P, PICKS, TOPK)),
                                       iota.unsqueeze(1).to_broadcast((P, PICKS, TOPK)), ALU.is_equal))
                    st(v.tensor_tensor(hot4, hot4, idx_cf[:, :, c, :].unsqueeze(2).to_broadcast((P, PH, TOPK, TOPK)),
                                       ALU.mult))
                    st(v.tensor_reduce(expert[:, c], hot, AX_X, ALU.add))
                st(v.scalar_tensor_tensor(expert[:, 0], expert[:, 0], float(NK), expert[:, 1], ALU.mult, ALU.add))
                if not is_first(t):
                    dve.wait_ge(idx_u_set.sem, idx_u_set.at(t - 1, 1))
                v.tensor_copy(idx, expert[:, 0]).then_inc(idx_ready.sem, 1)
                heads = lambda z: z.rearrange("p (h n) -> p h n", h=PH)
                v.tensor_tensor(heads(gate), top_s, top_s[:, :, 0:1].to_broadcast((P, PH, TOPK)), ALU.subtract)\
                 .then_inc(gate_shifted.sem, 1)
                dve.wait_ge(gate_exp.sem, gate_exp.at(t, 1))
                st(v.tensor_reduce(gsum, heads(gate), AX_X, ALU.add))
                st(v.reciprocal(gsum, gsum))
                st(v.tensor_tensor(heads(gate), heads(gate), gsum.unsqueeze(2).to_broadcast((P, PH, TOPK)), ALU.mult))

            def front(t, s, st, late):
                if s < MAPS:
                    if not late:
                        attention(t, s)
                    elif s > HEADS_A and s % 2:
                        mix(t, (s - HEADS_A) // 2, st)
                elif late:
                    if s == S_ONORM:
                        norm_o(t, st)
                    elif s == S_OT:
                        keep_oT(t)
                    elif s == S_PROJ:
                        residual(t)
                    elif s == S_HN:
                        norm_h(t, st)
                    elif S_HEAD0 <= s < S_IDX:
                        select(t, s - S_HEAD0, st)
                    elif s == S_IDX:
                        experts(t, st)

            def dot_row(t, p):
                dve.wait_ge(u_loaded[p % RU].sem, u_loaded[p % RU].at(t, p // RU + 1))
                row = u_ring[:, p % RU, :]
                v.tensor_tensor_reduce(out=row, in0=row, in1=hn_u, scale=1.0, scalar=0.0, op0=ALU.mult, op1=ALU.add,
                                       accum_out=dot[:, p:p + 1]).then_inc(u_used.sem, 1)

            def make_diag(t, q):
                if q >= 2:
                    dve.wait_ge(v_used.sem, v_used.at(t, QUAD * (q - 1)))
                elif not is_first(t):
                    dve.wait_ge(v_used.sem, v_used.at(t - 1, PICKS - QUAD * (1 - q)))
                v.tensor_tensor(diag[:, q % 2], ident[:, :].unsqueeze(1).to_broadcast((P, QUAD, P)),
                                act[:, QUAD * q:QUAD * (q + 1)].unsqueeze(2).to_broadcast((P, QUAD, P)), ALU.mult)\
                 .then_inc(diag_ready.sem, 1)

            def body(tf, tu, tv):
                st = Steps(dve, front_step, tf)
                if tv is not None:
                    make_diag(tv, 0)
                for s in range(SLOTS):
                    p = (s - PICK0) * QUAD
                    picks = range(p, p + QUAD) if tu is not None and p >= 0 else ()
                    for q in picks[:1]:
                        dot_row(tu, q)
                    if tf is not None:
                        front(tf, s, st, False)
                    for q in picks[1:]:
                        dot_row(tu, q)
                    if tv is not None and 0 <= s - PICK0 < PICKS // QUAD - 1:
                        make_diag(tv, s - PICK0 + 1)
                    if tf is not None:
                        front(tf, s, st, True)
                if tf is not None:
                    st.end()
                if tu is not None:
                    dve.wait_ge(gelu_done.sem, gelu_done.at(tu, 1))
                    v.tensor_tensor(act, dot, gate_u, ALU.mult).then_inc(act_ready.sem, 1)
                    dve.wait_ge(act_ready.sem, act_ready.at(tu, 1))
                if tf is not None:
                    v.tensor_copy(hn_u, hn).then_inc(handed.sem, 1)
                    v.tensor_copy(gate_u, gate).then_inc(handed.sem, 1)
                    dve.wait_ge(handed.sem, handed.at(tf, 2))
                if tv is not None:
                    dve.wait_ge(v_used.sem, v_used.at(tv, PICKS))
                    dve.wait_ge(h_back.sem, h_back.at(tv, 1))
                    v.tensor_tensor(y, pAcc.rearrange("p b n -> p (b n)"), y, ALU.add).then_inc(y_ready.sem, 1)
            iterations(dve, body)


def tables():
    pos = np.arange(SEQ, dtype=np.float32)
    inv_freq = np.float32(500000.0) ** (-np.arange(0, ROT, 2, dtype=np.float32) / np.float32(ROT))
    ang = (pos[:, None] * inv_freq[None, :]).astype(np.float32)
    dist = SEQ - P + np.arange(P)[:, None] - np.arange(MASK_W)[None, :]
    count = sum(((dist >= 0) & (dist % d == 0) & (dist <= w)).astype(np.int64) for w, d in PATTERNS)
    mask_a = np.where(count > 0, np.log(np.maximum(count, 1)) / SCALE, NEG).astype(np.float32)
    mask_b = np.where(dist >= 0, 0.0, NEG).astype(mybir.dt.np(BF16))
    return {"c_ident": np.eye(P, dtype=np.float32), "c_cos": np.cos(ang), "c_sin": np.sin(ang),
            "c_mask_a": mask_a, "c_mask_b": mask_b,
            "c_iota": np.broadcast_to(np.arange(TOPK, dtype=np.float32), (P, TOPK)).copy()}


NAMES = ("x", "attn_norm_g", "w_in", "q_norm_a", "k_norm_a", "out_norm_a", "q_norm_b", "k_norm_b",
         "lambda_q1", "lambda_k1", "lambda_q2", "lambda_k2", "out_norm_b", "w_out", "ffn_norm_g",
         "w_peer_q", "peer_sub_keys", "peer_u", "peer_v")


def kernel(**inputs):
    import concourse.bacc as bacc
    from concourse.bass_utils import run_bass_kernel_spmd

    nc = bacc.Bacc("TRN2", target_bir_lowering=False, num_devices=1)
    arrays, args = {}, []
    named = [(n, np.ascontiguousarray(np.asarray(inputs[n])[0])) for n in NAMES] + list(tables().items())
    for name, a in named:
        arrays[f"in_{name}"] = a
        args.append(nc.dram_tensor(f"in_{name}", a.shape, mybir.dt.from_np(a.dtype), kind="ExternalInput").ap())
    args.append(nc.dram_tensor("out_h", (SEQ, D), F32, kind="ExternalOutput").ap())
    hybrid_layer(nc, *args)
    r = run_bass_kernel_spmd(nc, [arrays], core_ids=[0])
    return r.results[0]["out_h"].reshape(1, SEQ, D)
```
